# Optimizing a Trainium2 kernel written in Bass

```python
import jax, jax.numpy as jnp
from jax import lax
import numpy as np

D_MODEL = 2048
BATCH = 1
SEQ = 256
DEPTH = 1

CHUNK = 64
N_MEM = 256
MIX_WIDTH = D_MODEL
W_A = MIX_WIDTH // 2
G_A = 8
GA_DIM = W_A // G_A
SGU_BLOCK = 128
W_B = MIX_WIDTH - W_A
H_B = 8
DH_B = W_B // H_B
Q_BLOCK = 128
X_HEADS = 4
X_DH = D_MODEL // X_HEADS
D_FF = 5632
EPS = 1e-6

kernel_name = "hybrid_sgu_stickbreak_macaron_block"

def rmsnorm(x, g):
    xf = x.astype(jnp.float32)
    y = xf * lax.rsqrt(jnp.mean(xf * xf, axis=-1, keepdims=True) + EPS)
    return (y * g.astype(jnp.float32)).astype(x.dtype)

def layernorm(x, g, b):
    xf = x.astype(jnp.float32)
    mu = jnp.mean(xf, axis=-1, keepdims=True)
    var = jnp.mean(jnp.square(xf - mu), axis=-1, keepdims=True)
    y = (xf - mu) * lax.rsqrt(var + EPS)
    return (y * g.astype(jnp.float32) + b.astype(jnp.float32)).astype(x.dtype)

def swiglu(x, w_in, w_out):
    gate, up = jnp.split(x @ w_in, 2, axis=-1)
    return (jax.nn.silu(gate) * up) @ w_out

def spatial_gating_unit(za, ln_g, ln_b, w_s, b_s):
    bsz, seq, _ = za.shape
    u, v = jnp.split(za, 2, axis=-1)
    v = layernorm(v.reshape(bsz, seq, G_A, GA_DIM),
                  ln_g.reshape(G_A, GA_DIM), ln_b.reshape(G_A, GA_DIM))
    v = v.reshape(bsz, seq // SGU_BLOCK, SGU_BLOCK, G_A, GA_DIM)
    cidx = jnp.arange(SGU_BLOCK) // CHUNK
    mask = cidx[None, :] <= cidx[:, None]
    w = jnp.where(mask[None], w_s, jnp.zeros((), w_s.dtype))
    mixed = jnp.einsum('gts,bnsgc->bntgc', w, v) + b_s.T[:, :, None]
    return u * mixed.reshape(bsz, seq, W_A)

def stick_breaking_attention(q, k, v):
    seq = q.shape[1]
    q = q * (DH_B ** -0.5)
    outs = []
    for i in range(seq // Q_BLOCK):
        end = (i + 1) * Q_BLOCK
        q_blk = q[:, i * Q_BLOCK:end]
        k_pre, v_pre = k[:, :end], v[:, :end]
        z = jnp.einsum('bqhd,bkhd->bhqk', q_blk, k_pre).astype(jnp.float32)
        t_pos = i * Q_BLOCK + jnp.arange(Q_BLOCK)
        s_pos = jnp.arange(end)
        causal = s_pos[None, :] < t_pos[:, None]
        log_beta = jax.nn.log_sigmoid(z)
        log_1m = jnp.where(causal, jax.nn.log_sigmoid(-z), 0.0)
        rest = lax.cumsum(log_1m, axis=3, reverse=True) - log_1m
        a = jnp.where(causal, jnp.exp(log_beta + rest), 0.0)
        outs.append(jnp.einsum('bhqk,bkhd->bqhd', a.astype(v.dtype), v_pre))
    return jnp.concatenate(outs, axis=1)

def memory_cross_attention(xn, memn, w_cq, w_ckv, w_co):
    bsz, seq, _ = xn.shape
    q = (xn @ w_cq).reshape(bsz, seq, X_HEADS, X_DH) * (X_DH ** -0.5)
    k, v = jnp.split(memn @ w_ckv, 2, axis=-1)
    k = k.reshape(bsz, N_MEM, X_HEADS, X_DH)
    v = v.reshape(bsz, N_MEM, X_HEADS, X_DH)
    s = jnp.einsum('bshd,bmhd->bhsm', q, k).astype(jnp.float32)
    p = jax.nn.softmax(s, axis=-1).astype(v.dtype)
    o = jnp.einsum('bhsm,bmhd->bshd', p, v).reshape(bsz, seq, D_MODEL)
    return o @ w_co

def setup_inputs(seed: int = 0) -> dict:
    key = jax.random.key(seed)
    ks = jax.random.split(key, 32)
    f32 = jnp.float32

    def w(k, shape, fan_in):
        return jax.random.normal(k, shape, f32) * (fan_in ** -0.5)

    def gain(k, shape):
        return 1.0 + 0.05 * jax.random.normal(k, shape, f32)

    L = DEPTH
    return {
        "x": jax.random.normal(ks[0], (BATCH, SEQ, D_MODEL), f32),
        "mem": jax.random.normal(ks[1], (BATCH, N_MEM, D_MODEL), f32),
        "ffn1_norm": gain(ks[2], (L, D_MODEL)),
        "ffn1_w_in": w(ks[3], (L, D_MODEL, 2 * D_FF), D_MODEL),
        "ffn1_w_out": w(ks[4], (L, D_FF, D_MODEL), D_FF),
        "mix_norm": gain(ks[5], (L, D_MODEL)),
        "w_mix_in": w(ks[6], (L, D_MODEL, 2 * W_A + 3 * W_B), D_MODEL),
        "ln_v_gain": gain(ks[7], (L, W_A)),
        "ln_v_bias": 0.02 * jax.random.normal(ks[8], (L, W_A), f32),
        "spatial_w": w(ks[9], (L, G_A, SGU_BLOCK, SGU_BLOCK), SGU_BLOCK),
        "spatial_b": 1.0 + 0.1 * jax.random.normal(ks[10], (L, G_A, SGU_BLOCK), f32),
        "gnorm_a": gain(ks[11], (L, W_A)),
        "gnorm_b": gain(ks[12], (L, W_B)),
        "w_mix_out": w(ks[13], (L, MIX_WIDTH, D_MODEL), MIX_WIDTH),
        "cross_norm": gain(ks[14], (L, D_MODEL)),
        "mem_norm": gain(ks[15], (L, D_MODEL)),
        "w_cq": w(ks[16], (L, D_MODEL, D_MODEL), D_MODEL),
        "w_ckv": w(ks[17], (L, D_MODEL, 2 * D_MODEL), D_MODEL),
        "w_co": w(ks[18], (L, D_MODEL, D_MODEL), D_MODEL),
        "ffn2_norm": gain(ks[19], (L, D_MODEL)),
        "ffn2_w_in": w(ks[20], (L, D_MODEL, 2 * D_FF), D_MODEL),
        "ffn2_w_out": w(ks[21], (L, D_FF, D_MODEL), D_FF),
        "final_norm": gain(ks[22], (D_MODEL,)),
    }

def reference(x, mem, ffn1_norm, ffn1_w_in, ffn1_w_out, mix_norm, w_mix_in,
              ln_v_gain, ln_v_bias, spatial_w, spatial_b, gnorm_a, gnorm_b,
              w_mix_out, cross_norm, mem_norm, w_cq, w_ckv, w_co,
              ffn2_norm, ffn2_w_in, ffn2_w_out, final_norm):
    bsz, seq, _ = x.shape
    h = x
    for l in range(DEPTH):
        h = h + 0.5 * swiglu(rmsnorm(h, ffn1_norm[l]), ffn1_w_in[l], ffn1_w_out[l])

        z = rmsnorm(h, mix_norm[l]) @ w_mix_in[l]
        za = jax.nn.gelu(z[..., :2 * W_A])
        q, k, v = jnp.split(z[..., 2 * W_A:], 3, axis=-1)
        y_a = spatial_gating_unit(za, ln_v_gain[l], ln_v_bias[l], spatial_w[l], spatial_b[l])
        y_b = stick_breaking_attention(q.reshape(bsz, seq, H_B, DH_B),
                                       k.reshape(bsz, seq, H_B, DH_B),
                                       v.reshape(bsz, seq, H_B, DH_B)).reshape(bsz, seq, W_B)
        y = jnp.concatenate([rmsnorm(y_a, gnorm_a[l]), rmsnorm(y_b, gnorm_b[l])], axis=-1)
        h = h + y @ w_mix_out[l]

        h = h + memory_cross_attention(rmsnorm(h, cross_norm[l]), rmsnorm(mem, mem_norm[l]),
                                       w_cq[l], w_ckv[l], w_co[l])

        h = h + 0.5 * swiglu(rmsnorm(h, ffn2_norm[l]), ffn2_w_in[l], ffn2_w_out[l])
    return rmsnorm(h, final_norm)


_drawn_inputs = setup_inputs


def setup_inputs(seed=0):
    import zlib

    import numpy as np

    out = dict(_drawn_inputs(seed))
    spreads = {}
    factors = {'ln_v_gain': 3.582,
     'ln_v_bias': 8.0,
     'cross_norm': 8.0,
     'mem_norm': 8.0,
     'ffn2_norm': 4.025}
    for name, (base, spread) in spreads.items():
        noise = np.random.default_rng([zlib.crc32(name.encode()), seed]).standard_normal(out[name].shape)
        drawn = base * np.exp(spread * noise) if base else spread * noise
        out[name] = __import__('jax').numpy.asarray(drawn.astype(out[name].dtype))
    for name, factor in factors.items():
        out[name] = (out[name] * factor).astype(out[name].dtype)
    return out
```

```python
from contextlib import ExitStack

import concourse.bass as bass
from concourse import mybir
from concourse.alu_op_type import AluOpType as ALU

P = 128
D = 2048
TOK = 256
FF = 5632
W_GROUP = 1024
HEADS_B = 8
EPS = 1e-6
CH = 512
NT = TOK // P
UK = 2
RING = 4
DC = D // CH
KT = D // P
U8 = KT // UK
FKT = FF // P
U22 = FKT // UK
FJ = FF // CH

FFN1_IN = 0
FFN1_OUT = FFN1_IN + 2 * FJ * U8
MIX_IN = FFN1_OUT + DC * U22
CKV = MIX_IN + 10 * U8
MIX_OUT = CKV + 2 * DC * U8
CQ = MIX_OUT + DC * U8
CO = CQ + DC * U8
FFN2_IN = CO + DC * U8
FFN2_OUT = FFN2_IN + 2 * FJ * U8
UNITS = FFN2_OUT + DC * U22

MIX_COLS = [1024, 1536, 0, 512, 2048, 3072, 2560, 3584, 4096, 4608]
CKV_COLS = [D + CH * c for c in range(DC)] + [CH * c for c in range(DC)]

FILLS = [("x", DC), ("hid1", FJ), ("h1", DC), ("ws", 1), ("mem", DC), ("qk", 4), ("ya0", 1), ("ya1", 1),
         ("ck0", 1), ("yb0", 1), ("ck1", 1), ("yb1", 1), ("ck2", 1), ("ck3", 1),
         ("h2", DC), ("cq", DC), ("h3", DC), ("hid2", FJ)]
PLAIN_FILLS = ("ws", "qk", "ck0", "ck1", "ck2", "ck3", "cq")

AUX = ["gain_x", "gains", "sgu0", "sgu1"]
for _j in range(4):
    AUX += [f"z{_j}", f"cum{_j}", f"av{_j}"]
AUX += ["s0", "pt0", "o0", "s1", "pt1", "o1", "s2", "pt2", "o2", "s3", "pt3", "o3"]

STATS = ["x", "h1", "ln0", "ln1", "mem", "ya", "yb", "h2", "h3", "out"]

SQUARES = [("x", DC), ("h1", DC), ("mem", DC), ("ya", 2), ("yb", 2), ("h2", DC), ("h3", DC), ("out", DC)]

GAIN_ROWS = [("ffn1_norm", 16), ("mix_norm", 16), ("gnorm_a", 8), ("gnorm_b", 8), ("cross_norm", 16),
             ("mem_norm", 16), ("ffn2_norm", 16), ("spatial_b", 8)]
GAIN_AT = {}
for _name, _rows in GAIN_ROWS:
    GAIN_AT[_name] = sum(r for _, r in GAIN_ROWS[:len(GAIN_AT)])
N_GAINS = sum(r for _, r in GAIN_ROWS)


STAGED = [("qk", 4), ("ck", DC), ("cq", DC)]
RESIDUAL = [("x", 1), ("h1", DC), ("h2", DC), ("h3", DC), ("out", DC)]
VALUES = [("bv", 2), ("cv", DC)]


def number(order, name, k=0):
    n = 0
    for other, count in order:
        if other == name:
            return n + k
        n += count
    raise KeyError(name)


def split_number(name, k=0):
    return number([f for f in FILLS if f[0] not in PLAIN_FILLS], name, k)


Y_FILLS = ["ya0", "ya1", "yb0", "yb1"]
Y_GAINS = [GAIN_AT["gnorm_a"], GAIN_AT["gnorm_a"] + 4, GAIN_AT["gnorm_b"], GAIN_AT["gnorm_b"] + 4]

CO_PAIR = ([(0, u) for u in range(U8 - 2)] + [(1, u) for u in range(U8 - 2)]
           + [(0, U8 - 2), (0, U8 - 1), (1, U8 - 2), (1, U8 - 1)])


def ring_distance(u, after_long):
    if u >= RING or not after_long:
        return RING
    return U22 % RING if u < U22 % RING else U22 % RING + RING


def slot_loads(base, slot):
    n, at = 0, 0
    while at < base:
        length = U22 if FFN1_OUT <= at < MIX_IN or at >= FFN2_OUT else U8
        n += len(range(slot, length, RING))
        at += length
    return n


def encoder_block(nc, x, mem, ffn1_norm, ffn1_w_in, ffn1_w_out, mix_norm, w_mix_in, ln_v_gain,
                  ln_v_bias, spatial_w, spatial_b, gnorm_a, gnorm_b, w_mix_out, cross_norm, mem_norm,
                  w_cq, w_ckv, w_co, ffn2_norm, ffn2_w_in, ffn2_w_out, final_norm, out):
    f32 = mybir.dt.float32
    f32r = mybir.dt.float32r
    ACT = mybir.ActivationFunctionType
    AX = mybir.AxisListType.X

    gain_dram = {
        "ffn1_norm": ffn1_norm, "mix_norm": mix_norm, "gnorm_a": gnorm_a, "gnorm_b": gnorm_b,
        "cross_norm": cross_norm, "mem_norm": mem_norm, "ffn2_norm": ffn2_norm, "spatial_b": spatial_b}

    ctx = ExitStack()
    with ctx:
        def sb(name, shape, dt=f32, scope=ctx):
            return scope.enter_context(nc.sbuf_tensor(name, shape, dt))

        def sem(name):
            return ctx.enter_context(nc.semaphore(name))

        h = sb("h", [P, NT, D])
        a_hi = sb("a_hi", [P, KT, TOK], f32r)
        a_lo = sb("a_lo", [P, KT, TOK], f32r)
        b_hi = sb("b_hi", [P, KT, TOK], f32r)
        b_lo = sb("b_lo", [P, KT, TOK], f32r)
        raw = sb("raw", [P, RING, UK, CH])
        w_hi = sb("w_hi", [P, RING, UK, CH], f32r)
        w_lo = sb("w_lo", [P, RING, UK, CH], f32r)
        stage = sb("stage", [P, NT, CH])
        memq = sb("memq", [P, NT, CH])
        junk = sb("junk", [P, NT, CH])
        row_gain = sb("row_gain", [P, 2, W_GROUP])
        ident = sb("ident", [P, P])
        tri = sb("tri", [P, P])
        ones = sb("ones", [P, P])
        gains_raw = sb("gains_raw", [P, P])
        gains = sb("gains", [P, N_GAINS])
        minus_half = sb("minus_half", [P, 8])
        sq = sb("sq", [P, len(STATS), NT, DC])
        tot = sb("tot", [P, len(STATS), 8])
        rstd = sb("rstd", [P, len(STATS), 8])
        bn = sb("bn", [P, 8, 6])
        mv = sb("mv", [P, 8, 2])
        nmax = sb("nmax", [P, NT])
        esum = sb("esum", [P, NT])
        with ExitStack() as region:
            hid_hi = sb("hid_hi", [P, FKT - KT, TOK], f32r, region)
            hid_lo = sb("hid_lo", [P, FKT - KT, TOK], f32r, region)
        with ExitStack() as region:
            qk_t = sb("qk_t", [P, 2 * HEADS_B, TOK], f32, region)
            uv = sb("uv", [P, NT, 2 * W_GROUP], f32, region)
            with ExitStack() as inner:
                vb = sb("vb", [P, NT, W_GROUP], f32, inner)
                z = sb("z", [P, 2, 384], f32, inner)
                sp = sb("sp", [P, 2, 384], f32, inner)
                ex = sb("ex", [P, 2, 384], f32, inner)
                ws_t = sb("ws_t", [P, 8, P], f32, inner)
            with ExitStack() as inner:
                cq_t = sb("cq_t", [P, 4, TOK], f32, inner)
                prob = sb("prob", [P, NT, TOK], f32, inner)
                prob_t = sb("prob_t", [P, NT, TOK], f32, inner)
        mem_k = qk_t
        mem_v = uv
        final_gain = row_gain[:].rearrange("p a n -> p (a n)").rearrange("p (a n) -> p a n", a=1)

        acc = ctx.enter_context(nc.psum_tensor("acc", [P, 2 * NT, CH], f32))
        tp = ctx.enter_context(nc.psum_tensor("tp", [P, 4, TOK], f32))
        aux = ctx.enter_context(nc.psum_tensor("aux", [P, 2, CH], f32))
        aux4 = aux[:].rearrange("p a (b n) -> p (a b) n", b=2)

        w_loaded = [sem(f"w_loaded{r}") for r in range(RING)]
        w_hi_done = sem("w_hi_done")
        w_lo_done = sem("w_lo_done")
        w_used = sem("w_used")
        t_full = sem("t_full")
        t_hi = sem("t_hi")
        t_read = sem("t_read")
        aux_full = sem("aux_full")
        aux_read = sem("aux_read")
        o_hi = sem("o_hi")
        x_in = [sem(f"x_in{q}") for q in range(DC)]
        gain_x_in = sem("gain_x_in")
        gains_in = sem("gains_in")
        ln_in = sem("ln_in")
        ws_in = sem("ws_in")
        mem_in = sem("mem_in")
        fin_in = sem("fin_in")
        consts = sem("consts")
        silu_done = sem("silu_done")
        hid_done = sem("hid_done")
        staged = sem("staged")
        gelu_done = sem("gelu_done")
        val_done = sem("val_done")
        res_done = sem("res_done")
        sq_done = sem("sq_done")
        stat_in = sem("stat_in")
        stat_out = sem("stat_out")
        v_norm = sem("v_norm")
        v_affine = sem("v_affine")
        ws_done = sem("ws_done")
        ya_done = sem("ya_done")
        qk_done = sem("qk_done")
        z_done = sem("z_done")
        log_done = sem("log_done")
        sp_done = sem("sp_done")
        sp_masked = sem("sp_masked")
        ex_done = sem("ex_done")
        exp_done = sem("exp_done")
        ex_masked = sem("ex_masked")
        yb_done = sem("yb_done")
        cq_done = sem("cq_done")
        nmax_done = sem("nmax_done")
        prob_exp = sem("prob_exp")
        prob_done = sem("prob_done")
        last_done = sem("last_done")
        out_act = sem("out_act")
        out_dve = sem("out_dve")
        out_stored = sem("out_stored")
        act_self = sem("act_self")
        dve_self = sem("dve_self")
        pool_self = sem("pool_self")

        block = ctx.enter_context(nc.Block())

        def stat(name):
            return STATS.index(name)

        def rate(u, length):
            return len(range(u % RING, length, RING))

        @block.sync
        def _(eng):
            def load(w, row, col, first, u, after_long=False, wait=True):
                if wait:
                    eng.wait_ge(w_lo_done, first + (u - ring_distance(u, after_long) + 1))
                src = w[row * UK * P:(row + 1) * UK * P, bass.ds(col, CH)]
                eng.dma_start(raw[:, u % RING], src.rearrange("(k p) n -> p k n", p=P)
                              ).then_inc(w_loaded[u % RING], 16)

            def chunk(w, col, first, after_long=False):
                for u in range(U8):
                    load(w, u, col, first, u, after_long)

            def ffn_in(w, base):
                for u in range(U8):
                    if base == FFN1_IN and u < DC:
                        eng.dma_start(h[:, :, u * CH:(u + 1) * CH],
                                      x[0, :, u * CH:(u + 1) * CH].rearrange("(t p) n -> p t n", p=P)
                                      ).then_inc(x_in[u], 16)
                    load(w, u, 0, base, u, wait=base != FFN1_IN or u >= RING)
                chunk(w, FF, base + U8)
                with eng.Fori(1, FJ) as j:
                    chunk(w, CH * j, base + 2 * U8 * j)
                    chunk(w, CH * j + FF, base + 2 * U8 * j + U8)

            def ffn_out(w, base):
                for u in range(U22):
                    load(w, u, 0, base, u)
                with eng.Fori(1, DC) as n:
                    for u in range(U22):
                        load(w, u, CH * n, base + U22 * n, u, after_long=True)

            ffn_in(ffn1_w_in[0], FFN1_IN)
            ffn_out(ffn1_w_out[0], FFN1_OUT)
            for c, col in enumerate(MIX_COLS):
                chunk(w_mix_in[0], col, MIX_IN + U8 * c, after_long=c == 0)
            for c, col in enumerate(CKV_COLS):
                chunk(w_ckv[0], col, CKV + U8 * c)
            for c in range(DC):
                chunk(w_mix_out[0], CH * c, MIX_OUT + U8 * c)
            for c in range(DC):
                chunk(w_cq[0], CH * c, CQ + U8 * c)
            for pos, (c, u) in enumerate(CO_PAIR):
                load(w_co[0], u, CH * c, CO, pos)
            for c in range(2, DC):
                chunk(w_co[0], CH * c, CO + U8 * c)
            ffn_in(ffn2_w_in[0], FFN2_IN)
            ffn_out(ffn2_w_out[0], FFN2_OUT)

            for n in range(DC):
                eng.wait_ge(out_act, n + 1)
                eng.wait_ge(out_dve, n + 1)
                eng.dma_start(out[0, :, n * CH:(n + 1) * CH].rearrange("(t p) n -> p t n", p=P),
                              h[:, :, n * CH:(n + 1) * CH]).then_inc(out_stored, 16)
            eng.wait_ge(out_stored, 16 * DC)

        @block.gpsimd
        def _(eng):
            steps = [0]

            def chain(ins):
                steps[0] += 1
                ins.then_inc(pool_self, 1)
                eng.wait_ge(pool_self, steps[0])

            chain(eng.memset(ident[:], 0.0))
            eng.affine_select(out=ident[:], in_=ident[:], compare_op=ALU.not_equal, fill=1.0, base=0,
                              pattern=[[-1, P]], channel_multiplier=1).then_inc(consts, 1)
            chain(eng.memset(ones[:], 1.0))
            eng.affine_select(out=tri[:], in_=ones[:], compare_op=ALU.is_ge, fill=0.0, base=0,
                              pattern=[[-1, P]], channel_multiplier=1).then_inc(consts, 1)
            chain(eng.memset(minus_half[:], -0.5))

            def rstd_of(name, n):
                k = stat(name)
                eng.wait_ge(stat_in, k + 1)
                eng.tensor_tensor(rstd[:, k, 0:n], tot[:, k, 0:n], minus_half[:, 0:n], ALU.pow
                                  ).then_inc(stat_out, 1)

            def affine(half):
                cols = slice(half * CH, (half + 1) * CH)
                v = uv[:, :, W_GROUP + half * CH:W_GROUP + (half + 1) * CH]
                eng.wait_ge(v_norm, half + 1)
                if half == 0:
                    eng.wait_ge(ln_in, 32)
                for t in range(NT):
                    last = eng.tensor_tensor(v[:, t], v[:, t], row_gain[:, 0, cols], ALU.mult)
                chain(last)
                for t in range(NT):
                    last = eng.tensor_tensor(v[:, t], v[:, t], row_gain[:, 1, cols], ALU.add)
                last.then_inc(v_affine, 1)

            def load_mem(q):
                if q:
                    eng.wait_ge(t_full, number(FILLS, "mem", q - 1) + 1)
                    eng.wait_ge(sq_done, number(SQUARES, "mem", q - 1) + 1)
                eng.dma_start(memq[:], mem[0, :, q * CH:(q + 1) * CH].rearrange("(t p) n -> p t n", p=P)
                              ).then_inc(mem_in, 16)

            rstd_of("x", NT)
            eng.dma_start(row_gain[:, 0], ln_v_gain[0:1, :].broadcast_to([P, W_GROUP])
                          ).then_inc(ln_in, 16)
            eng.dma_start(row_gain[:, 1], ln_v_bias[0:1, :].broadcast_to([P, W_GROUP])
                          ).then_inc(ln_in, 16)
            load_mem(0)
            eng.wait_ge(t_read, number(FILLS, "h1", 2) + 1)
            eng.dma_start(stage[:].rearrange("p t (g s) -> p (t g) s", s=P),
                          spatial_w[0].rearrange("g t s -> t g s")).then_inc(ws_in, 16)
            rstd_of("h1", NT)
            rstd_of("ln0", 8)
            load_mem(1)
            affine(0)
            rstd_of("ln1", 8)
            load_mem(2)
            affine(1)
            load_mem(3)
            eng.wait_ge(v_affine, 2)
            eng.dma_start(row_gain[:].rearrange("p a n -> p (a n)"),
                          final_norm.rearrange("(a n) -> a n", a=1).broadcast_to([P, D])
                          ).then_inc(fin_in, 16)
            rstd_of("mem", NT)
            rstd_of("ya", NT)
            for j in range(4):
                for src, ready, done in ((sp, sp_done, sp_masked), (ex, exp_done, ex_masked)):
                    eng.wait_ge(ready, j + 1)
                    for lo in (0, 2 * P):
                        blk = src[:, :, lo:lo + P]
                        last = eng.affine_select(out=blk, in_=blk, compare_op=ALU.is_gt, fill=0.0,
                                                 base=0, pattern=[[0, 2], [1, P]],
                                                 channel_multiplier=-1)
                    last.then_inc(done, 1)
            rstd_of("yb", NT)
            rstd_of("h2", NT)
            rstd_of("h3", NT)
            rstd_of("out", NT)

        @block.scalar
        def _(eng):
            steps = [0]

            def chain(ins):
                steps[0] += 1
                ins.then_inc(act_self, 1)
                eng.wait_ge(act_self, steps[0])

            def split(base, n, u, length=U8, after_long=False, wait=True):
                loads = slot_loads(base, u % RING) + u // RING + rate(u, length) * n
                eng.wait_ge(w_loaded[u % RING], 16 * loads + 16)
                if wait:
                    eng.wait_ge(w_used, base + length * n + (u - ring_distance(u, after_long) + 1))
                eng.activation(w_hi[:, u % RING], raw[:, u % RING], ACT.Copy).then_inc(w_hi_done, 1)

            def fill_hi(fill, dst, gain=None, src=tp):
                eng.wait_ge(t_full, fill + 1)
                if gain is None:
                    eng.activation(dst, src[:], ACT.Copy).then_inc(t_hi, 1)
                    return
                for i in range(4):
                    last = eng.activation(dst[:, i], src[:, i], ACT.Copy,
                                          scale=gains[:, bass.ds(gain + i, 1)])
                last.then_inc(t_hi, 1)

            def squares(name, n, src):
                if name != "x" or n > 0:
                    eng.wait_ge(sq_done, number(SQUARES, name) + n)
                for t in range(NT):
                    last = eng.activation(junk[:, t], src[:, t], ACT.Square,
                                          accum_out=sq[:, stat(name), t, bass.ds(n, 1)])
                last.then_inc(sq_done, 1)

            def residual_squares(name, n):
                eng.wait_ge(res_done, number(RESIDUAL, name) + n + 1)
                squares(name, n, h[:, :, bass.ds(CH * n, CH)])

            def to_stage(first, acc_at, rs, free):
                eng.wait_ge(w_used, first + U8)
                eng.wait_ge(t_full, free + 1)
                for t in range(NT):
                    last = eng.activation(stage[:, t], acc[:, NT * acc_at + t], ACT.Copy,
                                          scale=rstd[:, stat(rs), t:t + 1])
                last.then_inc(staged, 1)

            def ffn_in(base, rs, gate_first, hid, first_hi):
                def gate(j, hid_dst):
                    for u in range(U8):
                        split(base, 2 * j, u)
                        if u == 6:
                            fill_hi(number(FILLS, hid) - 1 + j, hid_dst)

                def up(j):
                    for u in range(U8):
                        split(base, 2 * j + 1, u)
                        if u == 3:
                            eng.wait_ge(stat_out, stat(rs) + 1)
                            eng.wait_ge(w_used, base + U8 + 2 * U8 * j)
                            for t in range(NT):
                                last = eng.activation(stage[:, t], acc[:, t], ACT.Silu,
                                                      scale=rstd[:, stat(rs), t:t + 1])
                            last.then_inc(silu_done, 1)

                gate_first()
                up(0)
                with eng.Fori(1, DC + 1) as j:
                    gate(j, first_hi[:, bass.ds(4 * j - 4, 4), :])
                    up(j)
                with eng.Fori(DC + 1, FJ) as j:
                    gate(j, hid_hi[:, bass.ds(4 * j - 4 - KT, 4), :])
                    up(j)

            def ffn_out(base, hid, name, h_hi, gain):
                for u in range(U22):
                    split(base, 0, u, U22)
                    if u == 6:
                        fill_hi(number(FILLS, hid, FJ - 1), hid_hi[:, FKT - KT - 4:FKT - KT])
                with eng.Fori(1, DC) as n:
                    for u in range(U22):
                        split(base, n, u, U22, after_long=True)
                        if u == 4:
                            eng.wait_ge(res_done, number(RESIDUAL, name) + n)
                            squares(name, n - 1, stage[:])
                        if u == 6 and h_hi is not None:
                            fill_hi(number(FILLS, name) - 1 + n,
                                    h_hi[:, bass.ds(4 * n - 4, 4), :], gain - 4 + 4 * n)

            def load_gains(names, done):
                for name, rows in names:
                    g = gain_dram[name]
                    src = g[0] if name == "spatial_b" else g[0].rearrange("(r p) -> r p", p=P)
                    eng.dma_start(gains_raw[GAIN_AT[name]:GAIN_AT[name] + rows, :], src
                                  ).then_inc(done, 16)

            load_gains(GAIN_ROWS[:1], gain_x_in)
            eng.wait_ge(consts, 2)
            eng.activation(nmax[:, 0:1], ones[:, 0:1], ACT.Copy).then_inc(act_self, 1)
            steps[0] += 1

            def first_gate_of_x():
                eng.wait_ge(aux_read, AUX.index("gain_x") + 1)
                at = {1: [0], 2: [1], 4: [2], 5: [3]}
                for u in range(U8):
                    if u == 4:
                        load_gains(GAIN_ROWS[1:], gains_in)
                    for q in at.get(u, []):
                        fill_hi(number(FILLS, "x", q), a_hi[:, 4 * q:4 * q + 4],
                                GAIN_AT["ffn1_norm"] + 4 * q, src=(tp, aux4)[q % 2])
                    split(FFN1_IN, 0, u, wait=u >= RING)
                    if u >= RING:
                        squares("x", u - RING, h[:, :, (u - RING) * CH:(u - RING + 1) * CH])

            ffn_in(FFN1_IN, "x", first_gate_of_x, "hid1", b_hi)
            ffn_out(FFN1_OUT, "hid1", "h1", a_hi, GAIN_AT["mix_norm"])

            for c in range(10):
                first = MIX_IN + U8 * c
                for u in range(U8):
                    split(MIX_IN, c, u, after_long=c == 0)
                    if u == 1 and 2 <= c <= 5:
                        fill_hi(number(FILLS, "mem", c - 2), b_hi[:, 4 * c - 8:4 * c - 4],
                                GAIN_AT["mem_norm"] + 4 * (c - 2))
                    if u == 1 and 5 <= c <= 6:
                        eng.wait_ge(ya_done, c - 4)
                        squares("ya", c - 5, uv[:, :, (c - 5) * CH:(c - 4) * CH])
                    if u == 2 and 1 <= c <= 4:
                        eng.wait_ge(mem_in, 16 * c)
                        squares("mem", c - 1, memq[:])
                    if u == 3 and 1 <= c <= 4:
                        if c == 1:
                            eng.wait_ge(stat_out, stat("h1") + 1)
                        eng.wait_ge(w_used, first)
                        col = MIX_COLS[c - 1]
                        for t in range(NT):
                            last = eng.activation(uv[:, t, col:col + CH],
                                                  acc[:, NT * ((c - 1) % 2) + t],
                                                  ACT.Gelu_apprx_tanh,
                                                  scale=rstd[:, stat("h1"), t:t + 1])
                        last.then_inc(gelu_done, 1)
                    if u == 3 and 5 <= c <= 8:
                        to_stage(first - U8, (c - 1) % 2, "h1",
                                 number(FILLS, "ws") if c == 5 else number(FILLS, "qk", c - 6))
                    if u == 4 and c == 0:
                        residual_squares("h1", DC - 1)
                    if u == 6 and c == 0:
                        fill_hi(number(FILLS, "h1", DC - 1), a_hi[:, 3 * 4:4 * 4],
                                GAIN_AT["mix_norm"] + 3 * 4)

            for c in range(2 * DC):
                first = CKV + U8 * c
                for u in range(U8):
                    split(CKV, c, u)
                    if u == 1 and 1 <= c <= 4:
                        eng.wait_ge(ex_done, c)
                        eng.activation(ex[:], ex[:], ACT.Exp).then_inc(exp_done, 1)
                    if u == 1 and c in (1, 6, 7):
                        q = {1: 1, 6: 2, 7: 3}[c]
                        fill_hi(number(FILLS, Y_FILLS[q]), a_hi[:, 4 * q:4 * q + 4], Y_GAINS[q])
                    if u == 2 and c == 3:
                        eng.wait_ge(yb_done, 2)
                        squares("yb", 0, vb[:, :, 0:CH])
                    if u == 3 and c >= DC + 1:
                        to_stage(first - U8, (c - 1) % 2, "mem",
                                 number(FILLS, "qk", 3) if c == DC + 1
                                 else number(FILLS, f"ck{c - DC - 2}"))
                    if u == 5 and c < 4:
                        eng.wait_ge(z_done, c + 1)
                        chain(eng.activation(sp[:], z[:], ACT.Abs))
                        chain(eng.activation(sp[:], sp[:], ACT.Exp, scale=-1.0))
                        eng.activation(sp[:], sp[:], ACT.Ln, bias=ones[:, 0:1]).then_inc(log_done, 1)
                    if u == 5 and c == 4:
                        eng.wait_ge(yb_done, 4)
                        squares("yb", 1, vb[:, :, CH:2 * CH])
                    if u == 6 and c == 0:
                        fill_hi(number(FILLS, Y_FILLS[0]), a_hi[:, 0:4], Y_GAINS[0])

            for c in range(DC):
                for u in range(U8):
                    split(MIX_OUT, c, u)
                    if u == 3 and c == 0:
                        to_stage(MIX_OUT - U8, 1, "mem", number(FILLS, "ck2"))
                    if u == 4 and c:
                        residual_squares("h2", c - 1)
                    if u == 6 and c:
                        fill_hi(number(FILLS, "h2", c - 1), b_hi[:, 4 * c - 4:4 * c],
                                GAIN_AT["cross_norm"] + 4 * (c - 1))

            def exponentials(head):
                eng.wait_ge(nmax_done, head + 1)
                for t in range(NT):
                    last = eng.activation(prob[:, t], aux4[:, t], ACT.Exp, bias=nmax[:, t:t + 1],
                                          accum_out=esum[:, t:t + 1])
                last.then_inc(prob_exp, 1)

            def head_out_hi(head):
                eng.wait_ge(aux_full, AUX.index(f"o{head}") + 1)
                eng.activation(a_hi[:, 4 * head:4 * head + 4], aux4, ACT.Copy).then_inc(o_hi, 1)

            for c in range(DC):
                for u in range(U8):
                    split(CQ, c, u)
                    if u == 1 and c >= 2:
                        exponentials(c - 2)
                    if u == 3 and c >= 1:
                        if c == 1:
                            eng.wait_ge(stat_out, stat("h2") + 1)
                        to_stage(CQ + U8 * (c - 1), (c - 1) % 2, "h2",
                                 number(FILLS, "ck3") if c == 1 else number(FILLS, "cq", c - 2))
                    if u == 4 and c >= 2:
                        head_out_hi(c - 2)
                    if u == 4 and c == 0:
                        residual_squares("h2", DC - 1)
                    if u == 6 and c == 0:
                        fill_hi(number(FILLS, "h2", DC - 1), b_hi[:, 3 * 4:4 * 4],
                                GAIN_AT["cross_norm"] + 3 * 4)

            for u in range(2 * U8):
                split(CO, 0, u)
                if u == 1:
                    exponentials(2)
                if u == 3:
                    to_stage(CQ + U8 * 3, 1, "h2", number(FILLS, "cq", 2))
                if u == 4:
                    head_out_hi(2)
                if u == U8 + 1:
                    exponentials(3)
                if u == U8 + 4:
                    head_out_hi(3)
            for c in range(2, DC):
                for u in range(U8):
                    split(CO, c, u)
                    if (c, u) == (3, 0):
                        fill_hi(number(FILLS, "h3", 1), b_hi[:, 4:8], GAIN_AT["ffn2_norm"] + 4)
                    if u == 3 and c == 2:
                        residual_squares("h3", 0)
                    if u == 4:
                        residual_squares("h3", c - 1)
                    if (c, u) == (2, 5):
                        fill_hi(number(FILLS, "h3", 0), b_hi[:, 0:4], GAIN_AT["ffn2_norm"])
                    if (c, u) == (3, 6):
                        fill_hi(number(FILLS, "h3", 2), b_hi[:, 8:12], GAIN_AT["ffn2_norm"] + 8)

            def first_gate_of_h3():
                for u in range(U8):
                    split(FFN2_IN, 0, u)
                    if u == 4:
                        residual_squares("h3", DC - 1)
                    if u == 6:
                        fill_hi(number(FILLS, "h3", 3), b_hi[:, 12:16], GAIN_AT["ffn2_norm"] + 12)

            ffn_in(FFN2_IN, "h3", first_gate_of_h3, "hid2", a_hi)
            ffn_out(FFN2_OUT, "hid2", "out", None, None)

            eng.wait_ge(res_done, number(RESIDUAL, "out", DC - 1) + 1)
            eng.wait_ge(sq_done, number(SQUARES, "out", DC - 1))
            eng.activation(junk[:, 0], h[:, 0, D - CH:D], ACT.Square,
                           accum_out=sq[:, stat("out"), 0, DC - 1:DC]).then_inc(sq_done, 1)
            eng.wait_ge(stat_out, stat("out") + 1)
            for n in range(DC):
                if n == DC - 1:
                    eng.wait_ge(last_done, 2)
                src = stage[:, 0] if n == DC - 1 else h[:, 0, n * CH:(n + 1) * CH]
                eng.activation(h[:, 0, n * CH:(n + 1) * CH], src, ACT.Copy,
                               scale=rstd[:, stat("out"), 0:1]).then_inc(out_act, 1)

        @block.vector
        def _(eng):
            steps = [0]

            def chain(ins):
                steps[0] += 1
                ins.then_inc(dve_self, 1)
                eng.wait_ge(dve_self, steps[0])

            def split(u, count):
                eng.wait_ge(w_hi_done, count + 1)
                eng.tensor_tensor(w_lo[:, u % RING], raw[:, u % RING], w_hi[:, u % RING].bitcast(f32),
                                  ALU.subtract).then_inc(w_lo_done, 1)

            def fill_lo(split_fill, dst, hi, gain=None, src=tp):
                eng.wait_ge(t_hi, split_fill + 1)
                if gain is None:
                    eng.tensor_tensor(dst, src[:], hi.bitcast(f32), ALU.subtract).then_inc(t_read, 1)
                    return
                for i in range(4):
                    last = eng.scalar_tensor_tensor(
                        out=dst[:, i], in0=src[:, i], scalar=gains[:, bass.ds(gain + i, 1)],
                        in1=hi[:, i].bitcast(f32), op0=ALU.mult, op1=ALU.subtract)
                last.then_inc(t_read, 1)

            def fill_copy(fill, dst, scale=1.0):
                eng.wait_ge(t_full, fill + 1)
                eng.tensor_scalar(dst, tp[:], scale, None, ALU.mult).then_inc(t_read, 1)

            def residual(done, acc_at, n, scale=1.0):
                eng.wait_ge(w_used, done)
                cols = h[:, :, bass.ds(CH * n, CH)]
                eng.scalar_tensor_tensor(out=cols, in0=acc[:, bass.ds(NT * acc_at, NT), :], scalar=scale,
                                         in1=cols, op0=ALU.mult, op1=ALU.add).then_inc(res_done, 1)

            def mean_square(name, quarters, width):
                eng.wait_ge(sq_done, number(SQUARES, name, quarters - 1) + 1)
                k = stat(name)
                chain(eng.tensor_reduce(out=tot[:, k, 0:NT], in_=sq[:, k, :, 0:quarters], axis=AX,
                                        op=ALU.add))
                eng.tensor_scalar(tot[:, k, 0:NT], tot[:, k, 0:NT], 1.0 / width, EPS, ALU.mult, ALU.add
                                  ).then_inc(stat_in, 1)

            def values(done, acc_at, rs, dst):
                eng.wait_ge(w_used, done)
                for t in range(NT):
                    last = eng.tensor_scalar(dst[:, t], acc[:, NT * acc_at + t],
                                             rstd[:, stat(rs), t:t + 1], None, ALU.mult)
                last.then_inc(val_done, 1)

            def ffn_in(base, rs, gate_first, hid, first_hi, first_lo):
                def hidden(j):
                    eng.wait_ge(silu_done, silus[base] + 1 + j)
                    eng.wait_ge(w_used, base + 2 * U8 + 2 * U8 * j)
                    for t in range(NT):
                        last = eng.scalar_tensor_tensor(
                            out=stage[:, t], in0=acc[:, NT + t], scalar=rstd[:, stat(rs), t:t + 1],
                            in1=stage[:, t], op0=ALU.mult, op1=ALU.mult)
                    last.then_inc(hid_done, 1)

                def gate(j, hi, lo):
                    for u in range(U8):
                        split(u, base + 2 * U8 * j + u)
                        if u == 3:
                            hidden(j - 1)
                        if u == 6:
                            fill_lo(split_number(hid) - 1 + j, lo, hi)

                def up(j):
                    for u in range(U8):
                        split(u, base + 2 * U8 * j + U8 + u)
                        if u == 0 and isinstance(j, int) and rs == "x":
                            mean_square("x", DC, D)
                        if u == 4 and isinstance(j, int) and rs == "x":
                            eng.wait_ge(aux_full, AUX.index("gains") + 1)
                            eng.tensor_copy(gains[:, GAIN_ROWS[0][1]:], aux[:, 0, GAIN_ROWS[0][1]:N_GAINS]
                                            ).then_inc(aux_read, 1)

                gate_first()
                up(0)
                with eng.Fori(1, DC + 1) as j:
                    gate(j, first_hi[:, bass.ds(4 * j - 4, 4), :], first_lo[:, bass.ds(4 * j - 4, 4), :])
                    up(j)
                with eng.Fori(DC + 1, FJ) as j:
                    gate(j, hid_hi[:, bass.ds(4 * j - 4 - KT, 4), :],
                         hid_lo[:, bass.ds(4 * j - 4 - KT, 4), :])
                    up(j)
                return hidden

            silus = {FFN1_IN: 0, FFN2_IN: FJ}

            def ffn_out(base, hidden, hid, name, hi, lo, gain):
                for u in range(U22):
                    split(u, base + u)
                    if u == 3:
                        hidden(FJ - 1)
                    if u == 6:
                        fill_lo(split_number(hid, FJ - 1), hid_lo[:, FKT - KT - 4:FKT - KT],
                                hid_hi[:, FKT - KT - 4:FKT - KT])
                if name == "out":
                    eng.wait_ge(fin_in, 16)
                with eng.Fori(1, DC) as n:
                    for u in range(U22):
                        split(u, base + U22 * n + u)
                        if u == 3:
                            eng.wait_ge(w_used, base + U22 * n)
                            eng.scalar_tensor_tensor(
                                out=stage[:], in0=acc[:, bass.ds(NT * ((n - 1) % 2), NT), :], scalar=0.5,
                                in1=h[:, :, bass.ds(CH * n - CH, CH)], op0=ALU.mult, op1=ALU.add
                                ).then_inc(res_done, 1)
                        if u == 5:
                            eng.wait_ge(res_done, number(RESIDUAL, name) + n)
                            cols = h[:, :, bass.ds(CH * n - CH, CH)]
                            if hi is not None:
                                eng.tensor_scalar(cols, stage[:], 1.0, None, ALU.mult)
                            for t in range(NT if hi is None else 0):
                                eng.tensor_tensor(cols[:, t:t + 1], stage[:, t:t + 1],
                                                  final_gain[:, :, bass.ds(CH * n - CH, CH)], ALU.mult)
                        if u == 6 and hi is not None:
                            fill_lo(split_number(name) - 1 + n, lo[:, bass.ds(4 * n - 4, 4), :],
                                    hi[:, bass.ds(4 * n - 4, 4), :], gain - 4 + 4 * n)

            eng.wait_ge(aux_full, AUX.index("gain_x") + 1)
            eng.tensor_copy(gains[:, 0:GAIN_ROWS[0][1]], aux[:, 0, 0:GAIN_ROWS[0][1]]
                            ).then_inc(aux_read, 1)
            eng.sem_inc(res_done, 1)

            def first_gate_of_x():
                at = {1: [0], 2: [1], 4: [2], 5: [3]}
                for u in range(U8):
                    for q in at.get(u, []):
                        fill_lo(split_number("x", q), a_lo[:, 4 * q:4 * q + 4],
                                a_hi[:, 4 * q:4 * q + 4], GAIN_AT["ffn1_norm"] + 4 * q,
                                src=(tp, aux4)[q % 2])
                    split(u, u)

            hidden = ffn_in(FFN1_IN, "x", first_gate_of_x, "hid1", b_hi, b_lo)
            ffn_out(FFN1_OUT, hidden, "hid1", "h1", a_hi, a_lo, GAIN_AT["mix_norm"])

            def normalise_v(half):
                v = uv[:, :, W_GROUP + half * CH:W_GROUP + (half + 1) * CH]
                k = stat(f"ln{half}")
                eng.wait_ge(gelu_done, half + 1)
                for t in range(NT):
                    for g in range(4):
                        last = eng.bn_stats(out=bn[:, 4 * t + g], in_=v[:, t, g * P:(g + 1) * P])
                chain(last)
                for i in range(8):
                    last = eng.bn_aggr(out=mv[:, i], in_=bn[:, i])
                chain(last)
                eng.tensor_scalar(tot[:, k, 0:8], mv[:, :, 1], 1.0, EPS, ALU.mult, ALU.add
                                  ).then_inc(stat_in, 1)

            def apply_v(half):
                v = uv[:, :, W_GROUP + half * CH:W_GROUP + (half + 1) * CH]
                k = stat(f"ln{half}")
                eng.wait_ge(stat_out, k + 1)
                for t in range(NT):
                    for g in range(4):
                        i = 4 * t + g
                        grp = v[:, t, g * P:(g + 1) * P]
                        last = eng.tensor_scalar(grp, grp, mv[:, i, 0:1], rstd[:, k, i:i + 1],
                                                 ALU.subtract, ALU.mult)
                last.then_inc(v_norm, 1)

            def gate_half(half):
                eng.wait_ge(aux_full, AUX.index(f"sgu{half}") + 1)
                eng.wait_ge(gelu_done, 3 + half)
                for g in range(4):
                    u = uv[:, :, (4 * half + g) * P:(4 * half + g + 1) * P]
                    m = aux4[:, g].rearrange("p (t c) -> p t c", t=NT)
                    at = GAIN_AT["spatial_b"] + 4 * half + g
                    last = eng.scalar_tensor_tensor(out=u, in0=m, scalar=gains[:, at:at + 1], in1=u,
                                                    op0=ALU.add, op1=ALU.mult)
                chain(last)
                eng.sem_inc(ya_done, 1)
                eng.sem_inc(aux_read, 1)

            for c in range(10):
                first = MIX_IN + U8 * c
                for u in range(U8):
                    split(u, first + u)
                    if u == 1 and 2 <= c <= 3:
                        apply_v(c - 2)
                    if u == 1 and 2 <= c <= 5:
                        g = 4 * (c - 2)
                        fill_lo(split_number("mem", c - 2), b_lo[:, g:g + 4], b_hi[:, g:g + 4],
                                GAIN_AT["mem_norm"] + g)
                    if u == 1 and c == 7:
                        eng.wait_ge(stat_out, stat("ya") + 1)
                        for t in range(NT):
                            y = uv[:, t, 0:W_GROUP]
                            last = eng.tensor_scalar(y, y, rstd[:, stat("ya"), t:t + 1], None, ALU.mult)
                        last.then_inc(ya_done, 1)
                    if u == 2 and c == 5:
                        mean_square("mem", DC, D)
                    if u == 2 and c == 6:
                        mean_square("ya", 2, W_GROUP)
                    if u == 3 and c == 0:
                        residual(MIX_IN, 1, DC - 1, 0.5)
                    if u == 3 and c == 9:
                        values(first, 0, "h1", vb[:, :, 0:CH])
                    if u == 5 and 1 <= c <= 2:
                        normalise_v(c - 1)
                    if u == 5 and 4 <= c <= 5:
                        gate_half(c - 4)
                    if u == 6 and c == 0:
                        mean_square("h1", DC, D)
                        fill_lo(split_number("h1", 3), a_lo[:, 12:16], a_hi[:, 12:16],
                                GAIN_AT["mix_norm"] + 12)
                    if u == 6 and c == 1:
                        eng.wait_ge(t_full, number(FILLS, "ws") + 1)
                        chain(eng.tensor_copy(ws_t[:], tp[:].rearrange("p a (b n) -> p (a b) n", b=2)))
                        eng.sem_inc(t_read, 1)
                        eng.memset(ws_t[64:P, :, 0:64], 0.0).then_inc(ws_done, 1)
                    if u == 6 and 5 <= c <= 8:
                        k = c - 5
                        at = (0, HEADS_B, 4, HEADS_B + 4)[k]
                        fill_copy(number(FILLS, "qk", k), qk_t[:, at:at + 4],
                                  (P ** -0.5) if k % 2 == 0 else 1.0)

            for c in range(2 * DC):
                first = CKV + U8 * c
                for u in range(U8):
                    split(u, first + u)
                    if u == 1 and 1 <= c <= 4:
                        eng.wait_ge(aux_full, AUX.index(f"cum{c - 1}") + 1)
                        chain(eng.tensor_tensor(ex[:], z[:], aux[:, :, 0:384], ALU.subtract))
                        eng.sem_inc(ex_done, 1)
                        eng.sem_inc(aux_read, 1)
                    if u == 1 and c in (1, 6, 7):
                        q = {1: 1, 6: 2, 7: 3}[c]
                        fill_lo(split_number(Y_FILLS[q]), a_lo[:, 4 * q:4 * q + 4],
                                a_hi[:, 4 * q:4 * q + 4], Y_GAINS[q])
                    if u == 1 and c == 5:
                        eng.wait_ge(stat_out, stat("yb") + 1)
                        for t in range(NT):
                            last = eng.tensor_scalar(vb[:, t], vb[:, t], rstd[:, stat("yb"), t:t + 1],
                                                     None, ALU.mult)
                        last.then_inc(yb_done, 1)
                    if u == 3 and 1 <= c <= 4:
                        eng.wait_ge(aux_full, AUX.index(f"av{c - 1}") + 1)
                        mixed = aux[:, 0].rearrange("p (a t d) -> p a t d", a=2, t=NT)
                        for t in range(NT):
                            dst = vb[:, t, 2 * P * (c - 1):2 * P * c].rearrange("p (a d) -> p a d", a=2)
                            last = eng.tensor_copy(dst, mixed[:, :, t])
                        chain(last)
                        eng.sem_inc(yb_done, 1)
                        eng.sem_inc(aux_read, 1)
                    if u == 3 and c == 0:
                        values(first, 1, "h1", vb[:, :, CH:2 * CH])
                    if u == 3 and 1 <= c <= DC:
                        values(first, (c - 1) % 2, "mem", mem_v[:, :, CH * (c - 1):CH * c])
                    if u == 5 and c < 4:
                        eng.wait_ge(aux_full, AUX.index(f"z{c}") + 1)
                        chain(eng.tensor_copy(z[:], aux[:, :, 0:384]))
                        eng.sem_inc(z_done, 1)
                        eng.sem_inc(aux_read, 1)
                    if u == 6 and c < 4:
                        eng.wait_ge(log_done, c + 1)
                        eng.scalar_tensor_tensor(out=sp[:], in0=z[:], scalar=0.0, in1=sp[:],
                                                 op0=ALU.max, op1=ALU.add).then_inc(sp_done, 1)
                    if u == 6 and c == 0:
                        fill_lo(split_number(Y_FILLS[0]), a_lo[:, 0:4], a_hi[:, 0:4], Y_GAINS[0])
                    if u == 6 and c == 4:
                        mean_square("yb", 2, W_GROUP)
                    if u == 6 and c > DC:
                        k = c - DC - 1
                        fill_copy(number(FILLS, f"ck{k}"), mem_k[:, 4 * k:4 * k + 4])

            for c in range(DC):
                first = MIX_OUT + U8 * c
                for u in range(U8):
                    split(u, first + u)
                    if u == 3 and c:
                        residual(first, (c - 1) % 2, c - 1)
                    if u == 6 and c == 0:
                        fill_copy(number(FILLS, "ck3"), mem_k[:, 12:16])
                    if u == 6 and c:
                        g = 4 * (c - 1)
                        fill_lo(split_number("h2", c - 1), b_lo[:, g:g + 4], b_hi[:, g:g + 4],
                                GAIN_AT["cross_norm"] + g)

            def row_maxima(head):
                eng.wait_ge(aux_full, AUX.index(f"s{head}") + 1)
                chain(eng.tensor_reduce(out=nmax[:], in_=aux4[:, 0:NT], axis=AX, op=ALU.max))
                eng.tensor_scalar(nmax[:], nmax[:], -1.0, None, ALU.mult).then_inc(nmax_done, 1)

            def normalise(head):
                eng.wait_ge(prob_exp, head + 1)
                chain(eng.reciprocal(esum[:], esum[:]))
                for t in range(NT):
                    last = eng.tensor_scalar(prob[:, t], prob[:, t], esum[:, t:t + 1], None, ALU.mult)
                chain(last)
                eng.sem_inc(prob_done, 1)
                eng.sem_inc(aux_read, 1)

            def copy_prob_t(head):
                eng.wait_ge(aux_full, AUX.index(f"pt{head}") + 1)
                eng.tensor_copy(prob_t[:], aux4[:, 2:4]).then_inc(aux_read, 1)

            def head_out_lo(head):
                eng.wait_ge(o_hi, head + 1)
                g = 4 * head
                eng.tensor_tensor(a_lo[:, g:g + 4], aux4, a_hi[:, g:g + 4].bitcast(f32), ALU.subtract
                                  ).then_inc(aux_read, 1)

            def copy_q_t(head):
                eng.wait_ge(t_full, number(FILLS, "cq", head) + 1)
                chain(eng.tensor_scalar(cq_t[:], tp[:], float(CH) ** -0.5, None, ALU.mult))
                eng.sem_inc(cq_done, 1)
                eng.sem_inc(t_read, 1)

            for c in range(DC):
                first = CQ + U8 * c
                for u in range(U8):
                    split(u, first + u)
                    if u == 0 and c >= 2:
                        row_maxima(c - 2)
                    if u == 1 and c >= 2:
                        normalise(c - 2)
                    if u == 3 and c >= 2:
                        copy_prob_t(c - 2)
                    if u == 4 and c >= 2:
                        head_out_lo(c - 2)
                    if u == 3 and c == 0:
                        residual(first, 1, DC - 1)
                    if u == 6 and c == 0:
                        mean_square("h2", DC, D)
                        fill_lo(split_number("h2", 3), b_lo[:, 12:16], b_hi[:, 12:16],
                                GAIN_AT["cross_norm"] + 12)
                    if u == 6 and c >= 1:
                        copy_q_t(c - 1)

            for u in range(2 * U8):
                split(u, CO + u)
                if u % U8 == 0:
                    row_maxima(2 + u // U8)
                if u % U8 == 1:
                    normalise(2 + u // U8)
                if u % U8 == 3:
                    copy_prob_t(2 + u // U8)
                if u % U8 == 4:
                    head_out_lo(2 + u // U8)
                if u == 6:
                    copy_q_t(3)
            for c in range(2, DC):
                for u in range(U8):
                    split(u, CO + U8 * c + u)
                    if (c, u) == (2, 1):
                        residual(CO + 2 * U8 - 2, 0, 0)
                    if (c, u) == (2, 3):
                        residual(CO + 2 * U8, 1, 1)
                    if (c, u) == (3, 3):
                        residual(CO + U8 * 3, 0, 2)
                    if (c, u) in ((2, 5), (3, 0), (3, 6)):
                        k = {(2, 5): 0, (3, 0): 1, (3, 6): 2}[c, u]
                        fill_lo(split_number("h3", k), b_lo[:, 4 * k:4 * k + 4],
                                b_hi[:, 4 * k:4 * k + 4], GAIN_AT["ffn2_norm"] + 4 * k)

            def first_gate_of_h3():
                for u in range(U8):
                    split(u, FFN2_IN + u)
                    if u == 3:
                        residual(FFN2_IN, 1, DC - 1)
                    if u == 6:
                        fill_lo(split_number("h3", 3), b_lo[:, 12:16], b_hi[:, 12:16],
                                GAIN_AT["ffn2_norm"] + 12)
                        mean_square("h3", DC, D)

            hidden = ffn_in(FFN2_IN, "h3", first_gate_of_h3, "hid2", a_hi, a_lo)
            ffn_out(FFN2_OUT, hidden, "hid2", "out", None, None, None)

            eng.wait_ge(w_used, UNITS)
            for t, done in ((0, res_done), (1, last_done)):
                c = h[:, t, D - CH:D]
                eng.scalar_tensor_tensor(out=c, in0=acc[:, NT + t], scalar=0.5, in1=c, op0=ALU.mult,
                                         op1=ALU.add).then_inc(done, 1)
            eng.wait_ge(last_done, 1)
            chain(eng.tensor_tensor_reduce(out=junk[:, 1], in0=c, in1=c, scale=1.0, scalar=0.0,
                                           op0=ALU.mult, op1=ALU.add,
                                           accum_out=sq[:, stat("out"), 1, DC - 1:DC]))
            mean_square("out", DC, D)
            eng.wait_ge(res_done, number(RESIDUAL, "out", DC - 1) + 1)
            for t in range(NT):
                last = eng.tensor_tensor(stage[:, t], h[:, t, D - CH:D], final_gain[:, 0, D - CH:D],
                                         ALU.mult)
            last.then_inc(last_done, 1)
            eng.wait_ge(last_done, 2)
            eng.wait_ge(stat_out, stat("out") + 1)
            for n in range(DC):
                src = stage[:, 1] if n == DC - 1 else h[:, 1, n * CH:(n + 1) * CH]
                eng.tensor_scalar(h[:, 1, n * CH:(n + 1) * CH], src, rstd[:, stat("out"), 1:2], None,
                                  ALU.mult).then_inc(out_dve, 1)

        @block.tensor
        def _(eng):
            def products(unit, slot, k_of, acc_at, start, stop):
                eng.wait_ge(w_lo_done, unit + 1)
                for i in range(UK):
                    x_hi, x_lo = k_of(i)
                    for t in range(NT):
                        dst = acc[:, bass.ds(NT * acc_at + t, 1), :]
                        rows = slice(t * P, (t + 1) * P)
                        eng.matmul(dst, x_hi[:, rows], w_hi[:, slot, i], start=start and i == 0,
                                   stop=False)
                        eng.matmul(dst, x_hi[:, rows], w_lo[:, slot, i], start=False, stop=False)
                        last = eng.matmul(dst, x_lo[:, rows], w_hi[:, slot, i], start=False,
                                          stop=stop and i == UK - 1)
                last.then_inc(w_used, 1)

            def unit_d(first, u, hi, lo, acc_at):
                products(first + u, u % RING,
                         lambda i: (hi[:, UK * u + i], lo[:, UK * u + i]), acc_at, u == 0, u == U8 - 1)

            def fill(srcs, dst=tp):
                for k in range(4):
                    for t in range(NT):
                        last = eng.transpose(dst[:, k, t * P:(t + 1) * P], srcs(k, t), ident[:])
                last.then_inc(t_full, 1)

            def from_stage(k, t):
                return stage[:, t, k * P:(k + 1) * P]

            def ffn_in(base, hi, lo, gate_first, hid):
                def up(j):
                    if not isinstance(j, int):
                        eng.wait_ge(hid_done, silus[base] + j)
                    for u in range(U8):
                        unit_d(base + 2 * U8 * j + U8, u, hi, lo, 1)

                gate_first()
                up(0)
                with eng.Fori(1, FJ) as j:
                    eng.wait_ge(silu_done, silus[base] + j)
                    for u in range(U8):
                        unit_d(base + 2 * U8 * j, u, hi, lo, 0)
                        if u == 2:
                            eng.wait_ge(hid_done, silus[base] + j)
                            eng.wait_ge(t_read, number(FILLS, hid) - 1 + j)
                            fill(from_stage)
                    up(j)

            silus = {FFN1_IN: 0, FFN2_IN: FJ}

            def ffn_out(base, in_base, hi, lo, hid, name, transposed):
                def k_tile(k):
                    return (hi[:, k], lo[:, k]) if k < KT else (hid_hi[:, k - KT], hid_lo[:, k - KT])

                def unit(n, u, acc_at):
                    products(base + U22 * n + u, u % RING, lambda i: k_tile(UK * u + i), acc_at,
                             u == 0, u == U22 - 1)

                eng.wait_ge(silu_done, silus[in_base] + FJ)
                for u in range(U22):
                    if u == U22 - 2:
                        eng.wait_ge(t_read, number(FILLS, hid, FJ - 1) + 1)
                    unit(0, u, 0)
                    if u == 2:
                        eng.wait_ge(hid_done, silus[in_base] + FJ)
                        eng.wait_ge(t_read, number(FILLS, hid, FJ - 1))
                        fill(from_stage)
                with eng.Fori(1, DC) as n:
                    eng.wait_ge(res_done, number(RESIDUAL, name) - 1 + n)
                    for u in range(U22):
                        unit(n, u, n % 2)
                        if u == 2 and transposed:
                            eng.wait_ge(res_done, number(RESIDUAL, name) + n)
                            eng.wait_ge(t_read, number(FILLS, name) - 1 + n)
                            fill(from_stage)

            def fill_h(name, res, n):
                eng.wait_ge(res_done, number(RESIDUAL, res, n) + 1)
                eng.wait_ge(t_read, number(FILLS, name, n))
                fill(lambda k, t: h[:, t, CH * n + k * P:CH * n + (k + 1) * P])

            def fill_stage(name, k, count):
                eng.wait_ge(staged, count)
                eng.wait_ge(t_read, number(FILLS, name, k))
                fill(from_stage)

            eng.wait_ge(consts, 2)
            eng.wait_ge(gain_x_in, 16)
            rows = GAIN_ROWS[0][1]
            eng.transpose(aux[:, 0, 0:rows], gains_raw[0:rows, :], ident[0:rows, 0:rows]
                          ).then_inc(aux_full, 1)

            def fill_x(q):
                eng.wait_ge(x_in[q], 16)
                if q == 1:
                    eng.wait_ge(aux_read, AUX.index("gain_x") + 1)
                if q >= 2:
                    eng.wait_ge(t_read, number(FILLS, "x", q - 2) + 1)
                fill(lambda k, t: h[:, t, CH * q + k * P:CH * q + (k + 1) * P], (tp, aux4)[q % 2])

            def first_gate_of_x():
                fill_x(0)
                fill_x(1)
                for u in range(U8):
                    if u in (2, 3):
                        fill_x(u)
                    if u % 2 == 0:
                        eng.wait_ge(t_read, number(FILLS, "x", u // 2) + 1)
                    unit_d(FFN1_IN, u, a_hi, a_lo, 0)
                eng.wait_ge(gains_in, 16 * len(GAIN_ROWS[1:]))
                eng.wait_ge(t_read, number(FILLS, "x", 3) + 1)
                eng.transpose(aux[:, 0, 0:N_GAINS], gains_raw[0:N_GAINS, :], ident[0:N_GAINS, 0:N_GAINS]
                              ).then_inc(aux_full, 1)

            ffn_in(FFN1_IN, a_hi, a_lo, first_gate_of_x, "hid1")
            ffn_out(FFN1_OUT, FFN1_IN, b_hi, b_lo, "hid1", "h1", True)

            for c in range(10):
                first = MIX_IN + U8 * c
                if c == 0:
                    eng.wait_ge(res_done, number(RESIDUAL, "h1", 2) + 1)
                if c == 1:
                    eng.wait_ge(res_done, number(RESIDUAL, "h1", 3) + 1)
                if 2 <= c <= 5:
                    eng.wait_ge(gelu_done, c - 1)
                if 6 <= c:
                    eng.wait_ge(staged, number(STAGED, "qk", c - 6) + 1)
                for u in range(U8):
                    if c == 0 and u % 2 == 0:
                        eng.wait_ge(t_read, number(FILLS, "h1", u // 2) + 1)
                    unit_d(first, u, a_hi, a_lo, c % 2)
                    if u == 1 and 4 <= c <= 5:
                        half = c - 4
                        eng.wait_ge(v_affine, half + 1)
                        eng.wait_ge(aux_read, AUX.index(f"sgu{half}"))
                        if half == 0:
                            eng.wait_ge(ws_done, 1)
                            eng.wait_ge(t_read, number(FILLS, "x", 3) + 1)
                        for g in range(4):
                            at = W_GROUP + (4 * half + g) * P
                            last = eng.matmul(aux4[:, g].rearrange("p (t c) -> p t c", t=NT),
                                              ws_t[:, 4 * half + g], uv[:, :, at:at + P],
                                              start=True, stop=True)
                        last.then_inc(aux_full, 1)
                    if u == 2 and c == 0:
                        fill_h("h1", "h1", DC - 1)
                    if u == 2 and c == 1:
                        eng.wait_ge(ws_in, 16)
                        eng.wait_ge(t_read, number(FILLS, "ws"))
                        ws = stage[:].rearrange("p t (g s) -> p (t g) s", s=P)
                        fill(lambda k, t: ws[:, 2 * k + t])
                    if u == 2 and 5 <= c <= 8:
                        fill_stage("qk", c - 5, number(STAGED, "qk", c - 5) + 1)
                    if u == 4 and 1 <= c <= 4:
                        eng.wait_ge(mem_in, 16 * c)
                        eng.wait_ge(t_read, number(FILLS, "mem", c - 1))
                        fill(lambda k, t: memq[:, t, k * P:(k + 1) * P])

            for c in range(2 * DC):
                first = CKV + U8 * c
                if c <= 5:
                    eng.wait_ge(val_done, c + 1)
                else:
                    eng.wait_ge(staged, number(STAGED, "ck", c - 6) + 1)
                for u in range(U8):
                    if c == 0 and u % 2 == 0:
                        eng.wait_ge(t_read, number(FILLS, "mem", u // 2) + 1)
                    unit_d(first, u, b_hi, b_lo, c % 2)
                    if u == 1 and c < 4:
                        if c % 2 == 0:
                            eng.wait_ge(t_read, number(FILLS, "qk", 3) + 1)
                        eng.wait_ge(aux_read, AUX.index(f"z{c}"))
                        for a in range(2):
                            q_t, k_t = qk_t[:, 2 * c + a], qk_t[:, HEADS_B + 2 * c + a]
                            eng.matmul(aux[:, a, 0:TOK], k_t[:, 0:P], q_t, start=True, stop=True)
                            last = eng.matmul(aux[:, a, TOK:384], k_t[:, P:TOK], q_t[:, P:TOK],
                                              start=True, stop=True)
                        last.then_inc(aux_full, 1)
                    if u == 5 and c < 4:
                        eng.wait_ge(sp_masked, c + 1)
                        eng.wait_ge(aux_read, AUX.index(f"cum{c}"))
                        for a in range(2):
                            eng.matmul(aux[:, a, 0:TOK], tri[:], sp[:, a, 0:TOK], start=True, stop=False)
                            eng.matmul(aux[:, a, P:TOK], ones[:], sp[:, a, TOK:384], start=False,
                                       stop=True)
                            last = eng.matmul(aux[:, a, TOK:384], tri[:], sp[:, a, TOK:384], start=True,
                                              stop=True)
                        last.then_inc(aux_full, 1)
                    if u == 7 and c < 4:
                        eng.wait_ge(ex_masked, c + 1)
                        eng.wait_ge(val_done, number(VALUES, "bv", 1) + 1)
                        eng.wait_ge(aux_read, AUX.index(f"av{c}"))
                        mixed = aux[:, 0].rearrange("p (a t d) -> p a t d", a=2, t=NT)
                        for a in range(2):
                            head = slice((2 * c + a) * P, (2 * c + a + 1) * P)
                            eng.matmul(mixed[:, a, 0], ex[:, a, 0:P], vb[:, 0, head], start=True,
                                       stop=True)
                            eng.matmul(mixed[:, a, 1], ex[:, a, P:TOK], vb[:, 0, head], start=True,
                                       stop=False)
                            last = eng.matmul(mixed[:, a, 1], ex[:, a, TOK:384], vb[:, 1, head],
                                              start=False, stop=True)
                        last.then_inc(aux_full, 1)
                    if (c, u) in ((0, 2), (0, 5)):
                        k0 = 0 if u == 2 else 4
                        eng.wait_ge(ya_done, 3)
                        eng.wait_ge(t_read, number(FILLS, Y_FILLS[k0 // 4]))
                        fill(lambda k, t: uv[:, t, (k0 + k) * P:(k0 + k + 1) * P])
                    if (c, u) in ((5, 5), (6, 5)):
                        k0 = 0 if c == 5 else 4
                        eng.wait_ge(yb_done, 5)
                        eng.wait_ge(t_read, number(FILLS, Y_FILLS[2 + k0 // 4]))
                        fill(lambda k, t: vb[:, t, (k0 + k) * P:(k0 + k + 1) * P])
                    if u == 2 and c > DC:
                        k = c - DC - 1
                        fill_stage(f"ck{k}", 0, number(STAGED, "ck", k) + 1)

            for c in range(DC):
                first = MIX_OUT + U8 * c
                if c < 2:
                    eng.wait_ge(staged, number(STAGED, "ck", 2 + c) + 1)
                else:
                    eng.wait_ge(res_done, number(RESIDUAL, "h2", c - 2) + 1)
                for u in range(U8):
                    if c == 0 and u % 2 == 0:
                        eng.wait_ge(t_read, number(FILLS, Y_FILLS[u // 2]) + 1)
                    unit_d(first, u, a_hi, a_lo, c % 2)
                    if u == 2 and c == 0:
                        fill_stage("ck3", 0, number(STAGED, "ck", 3) + 1)
                    if u == 2 and c:
                        fill_h("h2", "h2", c - 1)

            def scores(head):
                eng.wait_ge(cq_done, head + 1)
                eng.wait_ge(aux_read, AUX.index(f"s{head}"))
                for t in range(NT):
                    for k in range(4):
                        last = eng.matmul(aux4[:, t], cq_t[:, k, t * P:(t + 1) * P],
                                          mem_k[:, 4 * head + k], start=k == 0, stop=k == 3)
                last.then_inc(aux_full, 1)

            def transpose_probs(head):
                eng.wait_ge(prob_done, head + 1)
                for m in range(NT):
                    for t in range(NT):
                        last = eng.transpose(aux4[:, 2 + m, t * P:(t + 1) * P],
                                             prob[:, t, m * P:(m + 1) * P], ident[:])
                last.then_inc(aux_full, 1)

            def head_out(head):
                eng.wait_ge(aux_read, AUX.index(f"o{head}"))
                for k in range(4):
                    col = head * CH + k * P
                    for m in range(NT):
                        last = eng.matmul(aux4[:, k], mem_v[:, m, col:col + P], prob_t[:, m],
                                          start=m == 0, stop=m == NT - 1)
                last.then_inc(aux_full, 1)

            for c in range(DC):
                first = CQ + U8 * c
                if c < 2:
                    eng.wait_ge(res_done, number(RESIDUAL, "h2", 2 + c) + 1)
                else:
                    eng.wait_ge(staged, number(STAGED, "cq", c - 2) + 1)
                for u in range(U8):
                    if c == 0 and u % 2 == 0:
                        eng.wait_ge(t_read, number(FILLS, "h2", u // 2) + 1)
                    unit_d(first, u, b_hi, b_lo, c % 2)
                    if u == 0 and c >= 2:
                        head_out(c - 2)
                    if u == 2 and c == 0:
                        fill_h("h2", "h2", DC - 1)
                    if u == 2 and c >= 1:
                        fill_stage("cq", c - 1, number(STAGED, "cq", c - 1) + 1)
                    if u == 4 and c >= 1:
                        scores(c - 1)
                    if u == 7 and c >= 1:
                        transpose_probs(c - 1)

            eng.wait_ge(staged, number(STAGED, "cq", 2) + 1)
            for pos, (c, u) in enumerate(CO_PAIR):
                if (c, u) == (1, 0):
                    eng.wait_ge(staged, number(STAGED, "cq", 3) + 1)
                if u % 2 == 0:
                    eng.wait_ge(aux_read, AUX.index(f"o{u // 2}") + 1)
                products(CO + pos, pos % RING,
                         lambda i: (a_hi[:, UK * u + i], a_lo[:, UK * u + i]), c, u == 0, u == U8 - 1)
                if pos == 0:
                    head_out(2)
                if pos == 2:
                    fill_stage("cq", 3, number(STAGED, "cq", 3) + 1)
                if pos == 4:
                    scores(3)
                if pos == 7:
                    transpose_probs(3)
                if pos == 8:
                    head_out(3)
            for c in range(2, DC):
                eng.wait_ge(res_done, number(RESIDUAL, "h3", c - 2) + 1)
                for u in range(U8):
                    unit_d(CO + U8 * c, u, a_hi, a_lo, c % 2)
                    if (c, u) in ((2, 1), (2, 4), (3, 2)):
                        fill_h("h3", "h3", {(2, 1): 0, (2, 4): 1, (3, 2): 2}[c, u])

            def first_gate_of_h3():
                eng.wait_ge(res_done, number(RESIDUAL, "h3", 2) + 1)
                for u in range(U8):
                    if u % 2 == 0:
                        eng.wait_ge(t_read, number(FILLS, "h3", u // 2) + 1)
                    unit_d(FFN2_IN, u, b_hi, b_lo, 0)
                    if u == 2:
                        fill_h("h3", "h3", DC - 1)

            ffn_in(FFN2_IN, b_hi, b_lo, first_gate_of_h3, "hid2")
            ffn_out(FFN2_OUT, FFN2_IN, a_hi, a_lo, "hid2", "out", False)


INPUTS = ["x", "mem", "ffn1_norm", "ffn1_w_in", "ffn1_w_out", "mix_norm", "w_mix_in", "ln_v_gain",
          "ln_v_bias", "spatial_w", "spatial_b", "gnorm_a", "gnorm_b", "w_mix_out", "cross_norm",
          "mem_norm", "w_cq", "w_ckv", "w_co", "ffn2_norm", "ffn2_w_in", "ffn2_w_out", "final_norm"]


def kernel(**inputs):
    import numpy as np
    import concourse.bacc as bacc
    from concourse.bass_utils import run_bass_kernel_spmd

    nc = bacc.Bacc("TRN2", target_bir_lowering=False, num_devices=1)
    arrays, args = {}, []
    for name in INPUTS:
        a = np.ascontiguousarray(inputs[name])
        arrays["in_" + name] = a
        args.append(nc.dram_tensor("in_" + name, a.shape, mybir.dt.from_np(a.dtype),
                                   kind="ExternalInput").ap())
    out = nc.dram_tensor("out_h", (1, TOK, D), mybir.dt.float32, kind="ExternalOutput").ap()
    encoder_block(nc, *args, out)
    result = run_bass_kernel_spmd(nc, [arrays], core_ids=[0])
    return result.results[0]["out_h"]
```
